# Optimizing a Trainium2 kernel written in Bass

```python
import jax, jax.numpy as jnp
from jax import lax
import numpy as np

D_MODEL = 1024
BATCH = 1
SEQ = 1024
DEPTH = 1

POOL_WIDTH = D_MODEL // 2
POOL_WINDOWS = (2, 4, 8, 16)
POOL_GROUP = POOL_WIDTH // len(POOL_WINDOWS)
LRU_WIDTH = D_MODEL - POOL_WIDTH
LRU_HEADS = 8
LRU_HEAD_DIM = LRU_WIDTH // LRU_HEADS
CONV_WIDTH = 4
LRU_C = 8.0
MIX_WIDTH = POOL_WIDTH + LRU_WIDTH
IN_WIDTH = POOL_WIDTH + 2 * LRU_WIDTH
D_FF = ((8 * D_MODEL // 3 + 255) // 256) * 256
EPS = 1e-6

kernel_name = "hymba_pool_rglru_block"

def rmsnorm(x, g):
    xf = x.astype(jnp.float32)
    y = xf * lax.rsqrt(jnp.mean(xf * xf, axis=-1, keepdims=True) + EPS)
    return (y * g.astype(jnp.float32)).astype(x.dtype)

def pool_mixer(u, pool_w, pool_scale):
    B, S, _ = u.shape
    uf = u.astype(jnp.float32)
    pos = jnp.arange(1, S + 1, dtype=jnp.float32)[None, :, None]
    outs = []
    for g, w in enumerate(POOL_WINDOWS):
        ug = uf[..., g * POOL_GROUP:(g + 1) * POOL_GROUP]
        cs = jnp.cumsum(ug, axis=1)
        lag = jnp.pad(cs[:, :S - w], ((0, 0), (w, 0), (0, 0)))
        mean = (cs - lag) / jnp.minimum(pos, float(w))
        outs.append(mean - ug)
    d = jnp.stack(outs, axis=2)
    y = jnp.einsum('bsgc,gcd->bsgd', d, pool_w.astype(jnp.float32)).reshape(B, S, POOL_WIDTH)
    return (y * pool_scale.astype(jnp.float32)).astype(u.dtype)

def causal_depthwise_conv(u, w, b):
    C = u.shape[-1]
    y = lax.conv_general_dilated(
        u, w[:, None, :].astype(u.dtype), window_strides=(1,),
        padding=[(CONV_WIDTH - 1, 0)], dimension_numbers=('NWC', 'WIO', 'NWC'),
        feature_group_count=C)
    return y + b.astype(u.dtype)

def _lin_combine(c1, c2):
    a1, b1 = c1
    a2, b2 = c2
    return a1 * a2, a2 * b1 + b2

def rg_lru(xc, w_a, b_a, w_i, b_i, lam):
    B, S, C = xc.shape
    xf = xc.astype(jnp.float32)
    xh = xf.reshape(B, S, LRU_HEADS, LRU_HEAD_DIM)
    r = jax.nn.sigmoid(jnp.einsum('bshc,hcd->bshd', xh, w_a.astype(jnp.float32)).reshape(B, S, C) + b_a.astype(jnp.float32))
    i = jax.nn.sigmoid(jnp.einsum('bshc,hcd->bshd', xh, w_i.astype(jnp.float32)).reshape(B, S, C) + b_i.astype(jnp.float32))
    log_a = -LRU_C * r * jax.nn.softplus(-lam.astype(jnp.float32))
    a = jnp.exp(log_a)
    mult = jnp.sqrt(jnp.maximum(-jnp.expm1(2.0 * log_a), 0.0))
    bterm = mult * (i * xf)
    _, h = lax.associative_scan(_lin_combine, (a, bterm), axis=1)
    return h.astype(xc.dtype)

def setup_inputs(seed: int = 0) -> dict:
    key = jax.random.key(seed)
    ks = jax.random.split(key, 24)
    f32 = jnp.float32

    def nrm(k, shape, fan_in):
        return jax.random.normal(k, shape, f32) * (fan_in ** -0.5)

    def gain(k, shape):
        return 1.0 + 0.05 * jax.random.normal(k, shape, f32)

    x = jax.random.normal(ks[0], (BATCH, SEQ, D_MODEL), f32)
    ln1_g = gain(ks[1], (DEPTH, D_MODEL))
    w_in = nrm(ks[2], (DEPTH, D_MODEL, IN_WIDTH), D_MODEL)
    pool_w = nrm(ks[3], (DEPTH, len(POOL_WINDOWS), POOL_GROUP, POOL_GROUP), POOL_GROUP)
    pool_scale = 1.0 + 0.1 * jax.random.normal(ks[4], (DEPTH, POOL_WIDTH), f32)
    conv_w = nrm(ks[5], (DEPTH, CONV_WIDTH, LRU_WIDTH), CONV_WIDTH)
    conv_b = 0.02 * jax.random.normal(ks[6], (DEPTH, LRU_WIDTH), f32)
    w_a = nrm(ks[7], (DEPTH, LRU_HEADS, LRU_HEAD_DIM, LRU_HEAD_DIM), LRU_HEAD_DIM)
    b_a = 0.02 * jax.random.normal(ks[8], (DEPTH, LRU_WIDTH), f32)
    w_i = nrm(ks[9], (DEPTH, LRU_HEADS, LRU_HEAD_DIM, LRU_HEAD_DIM), LRU_HEAD_DIM)
    b_i = 0.02 * jax.random.normal(ks[10], (DEPTH, LRU_WIDTH), f32)
    u = jax.random.uniform(ks[11], (DEPTH, LRU_WIDTH), f32, minval=0.9, maxval=0.999)
    s = u ** (1.0 / LRU_C)
    lam = jnp.log(s) - jnp.log1p(-s)
    gn_pool_g = gain(ks[12], (DEPTH, POOL_WIDTH))
    gn_lru_g = gain(ks[13], (DEPTH, LRU_WIDTH))
    w_out = nrm(ks[14], (DEPTH, MIX_WIDTH, D_MODEL), MIX_WIDTH)
    ln2_g = gain(ks[15], (DEPTH, D_MODEL))
    w_ffn_gate = nrm(ks[16], (DEPTH, D_MODEL, D_FF), D_MODEL)
    w_ffn_up = nrm(ks[17], (DEPTH, D_MODEL, D_FF), D_MODEL)
    w_ffn_down = nrm(ks[18], (DEPTH, D_FF, D_MODEL), D_FF)
    lnf_g = gain(ks[19], (D_MODEL,))
    return {"x": x, "ln1_g": ln1_g, "w_in": w_in, "pool_w": pool_w, "pool_scale": pool_scale,
            "conv_w": conv_w, "conv_b": conv_b, "w_a": w_a, "b_a": b_a, "w_i": w_i, "b_i": b_i,
            "lam": lam, "gn_pool_g": gn_pool_g, "gn_lru_g": gn_lru_g, "w_out": w_out,
            "ln2_g": ln2_g, "w_ffn_gate": w_ffn_gate, "w_ffn_up": w_ffn_up,
            "w_ffn_down": w_ffn_down, "lnf_g": lnf_g}

def reference(x, ln1_g, w_in, pool_w, pool_scale, conv_w, conv_b, w_a, b_a, w_i, b_i,
              lam, gn_pool_g, gn_lru_g, w_out, ln2_g, w_ffn_gate, w_ffn_up, w_ffn_down, lnf_g):
    h = x
    for l in range(DEPTH):
        n = rmsnorm(h, ln1_g[l])
        proj = n @ w_in[l]
        u_pool = proj[..., :POOL_WIDTH]
        u_lru = proj[..., POOL_WIDTH:POOL_WIDTH + LRU_WIDTH]
        u_gate = proj[..., POOL_WIDTH + LRU_WIDTH:]
        y_pool = pool_mixer(u_pool, pool_w[l], pool_scale[l])
        xc = causal_depthwise_conv(u_lru, conv_w[l], conv_b[l])
        y_lru = rg_lru(xc, w_a[l], b_a[l], w_i[l], b_i[l], lam[l]) * jax.nn.gelu(u_gate)
        mix = jnp.concatenate([rmsnorm(y_pool, gn_pool_g[l]), rmsnorm(y_lru, gn_lru_g[l])], axis=-1)
        h = h + mix @ w_out[l]
        n2 = rmsnorm(h, ln2_g[l])
        h = h + (jax.nn.silu(n2 @ w_ffn_gate[l]) * (n2 @ w_ffn_up[l])) @ w_ffn_down[l]
    return rmsnorm(h, lnf_g)


_drawn_inputs = setup_inputs


def setup_inputs(seed=0):
    import zlib

    import numpy as np

    out = dict(_drawn_inputs(seed))
    spreads = {}
    factors = {'b_a': 21.86, 'b_i': 8.0}
    for name, (base, spread) in spreads.items():
        noise = np.random.default_rng([zlib.crc32(name.encode()), seed]).standard_normal(out[name].shape)
        drawn = base * np.exp(spread * noise) if base else spread * noise
        out[name] = __import__('jax').numpy.asarray(drawn.astype(out[name].dtype))
    for name, factor in factors.items():
        out[name] = (out[name] * factor).astype(out[name].dtype)
    return out
```

```python
from contextlib import ExitStack

import concourse.bass as bass
from concourse import mybir

F32 = mybir.dt.float32
F32R = mybir.dt.float32r
ALU = mybir.AluOpType
ACT = mybir.ActivationFunctionType

P = 128
KIB = 1024


def hymba_pool_rglru_block(nc, x, ln1_g, w_in, pool_w, pool_scale, conv_w, conv_b, w_a, b_a, w_i, b_i,
                           lam, gn_pool_g, gn_lru_g, w_out, ln2_g, w_gate, w_up, w_down, lnf_g, out):
    S, D = x.shape[1], x.shape[2]
    HALF = S // 2
    TT = S // P
    KT = D // P
    GW = pool_w.shape[1] * pool_w.shape[2]
    GT = GW // P
    TAPS = conv_w.shape[1]
    HD = w_a.shape[2]
    F = w_gate.shape[2]
    FT = F // P
    CH = 2
    NCH = FT // CH
    NH = D // 512
    PAD = 16
    WINDOWS = (2, 4, 8, 16)
    EPS = 1e-6
    LRU_C = 8.0
    COLS = list(range(GT, 2 * GT)) + list(range(GT)) + list(range(2 * GT, 3 * GT))
    NC_IN = len(COLS)
    POOL0, GATE0 = GT, 2 * GT

    xf = x.rearrange("b s d -> (b s) d")
    outf = out.rearrange("b s d -> (b s) d")
    w_in_v = w_in[0].rearrange("(k p) n -> p k n", p=P)
    w_out_v = w_out[0].rearrange("(k p) n -> p k n", p=P)
    w_gate_v = w_gate[0].rearrange("(k p) n -> p k n", p=P)
    w_up_v = w_up[0].rearrange("(k p) n -> p k n", p=P)
    w_down_v = w_down[0].rearrange("(f p) n -> p f n", p=P)

    with ExitStack() as ctx:
        BASE = (nc.sbuf_base + 255) // 256 * 256
        ctx.enter_context(nc.sbuf_tensor("arena", [P, 207 * 256], F32))

        def at(name, kib, shape, dt=F32):
            return nc.alloc_sbuf_tensor_at(name, shape, dt, offset=BASE + int(kib * KIB))

        h = at("h", 0, [P, TT, D])
        nT_hi = at("nT_hi", 32, [P, KT, S], F32R)
        nT_lo = at("nT_lo", 64, [P, KT, S], F32R)
        w_raw = at("w_raw", 96, [P, 2, KT, P])
        w_hi = [at(f"w_hi{s}", 104 + 4 * s, [P, KT, P], F32R) for s in range(2)]
        w_lo = [at(f"w_lo{s}", 112 + 4 * s, [P, KT, P], F32R) for s in range(2)]
        xc = [at(f"xc{s}", 120 + 4 * s, [P, S]) for s in range(2)]
        sumA = at("sumA", 128, [P, PAD + S])
        sumB = at("sumB", 132.125, [P, PAD + S])
        rg = at("rg", 136.25, [P, S])
        ig = at("ig", 140.25, [P, S])
        ag = at("ag", 144.25, [P, S])
        t2b = at("t2b", 148.25, [P, S])
        y = [at(f"y{g}", 152.25 + 16 * g, [P, GT, S]) for g in range(2)]
        gate_w = [at(f"gate_w{g}", 184.25 + 2 * g, [P, GT, P]) for g in range(2)]
        pool_ws = at("pool_ws", 188.25, [P, GT, P])
        ub = [at(f"ub{s}", 190.25 + 4.125 * s, [P, PAD + S]) for s in range(2)]
        wo_hi = [at(f"wo_hi{s}", 120 + 16 * s, [P, GT, 512], F32R) for s in range(2)]
        wo_lo = [at(f"wo_lo{s}", 128 + 16 * s, [P, GT, 512], F32R) for s in range(2)]
        xs2 = [at(f"xs2_{s}", 108 + 8 * s, [P, D]) for s in range(2)]
        dn_raw = at("dn_raw", 96, [P, CH, D])
        dn_hi = at("dn_hi", 104, [P, CH, D], F32R)
        dn_lo = at("dn_lo", 112, [P, CH, D], F32R)
        gu_hi = [at(f"gu_hi{s}", 120 + 16 * s, [P, 2, KT, P], F32R) for s in range(CH)]
        gu_lo = [at(f"gu_lo{s}", 128 + 16 * s, [P, 2, KT, P], F32R) for s in range(CH)]
        gu_raw = [at(f"gu_raw{s}", 152.25 + 8 * s, [P, 2, KT, P]) for s in range(CH)]
        hT_hi = at("hT_hi", 168.25, [P, CH, S], F32R)
        hT_lo = at("hT_lo", 176.25, [P, CH, S], F32R)
        silu = [at(f"silu{s}", 184.25 + 2 * s, [P, HALF]) for s in range(2)]
        hf = [at(f"hf{s}", 188.25 + 2 * s, [P, HALF]) for s in range(2)]
        fin = [at(f"fin{m}", 32 + 4 * m, [P, D]) for m in range(TT)]
        fin_sq = at("fin_sq", 64, [P, D])
        g_row = at("g_row", 198.5, [P, D])
        ident = at("ident", 202.5, [P, P])
        vec = at("vec", 203, [P, 64])
        invp = at("invp", 203.25, [P, PAD])
        ones = at("ones", 203.375, [P, 8])
        ssq = at("ssq", 203.5, [P, 3 * TT])
        var = at("var", 203.75, [P, 3 * TT])
        sd = at("sd", 204, [P, 3 * TT])
        rstd = at("rstd", 204.25, [P, 3 * TT])
        tmp = at("tmp", 204.5, [P, 3 * TT])
        gvar = at("gvar", 204.75, [P, 2 * TT])
        gsd = at("gsd", 205, [P, 2 * TT])
        grstd = at("grstd", 205.25, [P, 2 * TT])
        sp = at("sp", 205.5, [P, 8, GT])
        dfix = at("dfix", 205.75, [P, PAD])
        early = at("early", 205.875, [P, 8])
        vrows = at("vrows", 206, [P, P])

        psum = [ctx.enter_context(nc.psum_tensor(f"bank{b}", [P, 512], F32)) for b in range(8)]
        pj, pg, pt = psum[0:4], psum[4:6], psum[6:8]

        def sem(name):
            return ctx.enter_context(nc.semaphore(name))

        x_in = [sem(f"x_in{t}") for t in range(TT)]
        rows_in, grow_in, small_in = sem("rows_in"), sem("grow_in"), sem("small_in")
        w_in_slot = [sem(f"w_in_slot{s}") for s in range(2)]
        wo_in, dn_in = sem("wo_in"), sem("dn_in")
        gu_in = [sem(f"gu_in{s}") for s in range(CH)]
        stored = sem("stored")
        consts = sem("consts")
        zeroed = sem("zeroed")
        w_lo_ok = sem("w_lo_ok")
        fin_g_ok = sem("fin_g_ok")
        ix_ok = sem("ix_ok")
        ssum_ok = sem("ssum_ok")
        dn_lo_ok, gu_lo_ok = sem("dn_lo_ok"), sem("gu_lo_ok")
        sq_ok = sem("sq_ok")
        sd_ok = sem("sd_ok")
        n_hi_ok = sem("n_hi_ok")
        w_hi_ok = sem("w_hi_ok")
        exp_ok = sem("exp_ok")
        vec_ok = sem("vec_ok")
        u_ok = sem("u_ok")
        gate_evac = sem("gate_evac")
        t2_ok = sem("t2_ok")
        sqrt_ok = sem("sqrt_ok")
        fin_n_ok = sem("fin_n_ok")
        psq_ok = sem("psq_ok")
        lsq_ok = sem("lsq_ok")
        ys_hi_ok, wo_hi_ok = sem("ys_hi_ok"), sem("wo_hi_ok")
        dn_hi_ok, gu_hi_ok = sem("dn_hi_ok"), sem("gu_hi_ok")
        silu_ok, hT_hi_ok = sem("silu_ok"), sem("hT_hi_ok")
        a_ok = sem("a_ok")
        dve_step = sem("dve_step")
        abs_ok, decay_ok = sem("abs_ok"), sem("decay_ok")
        var_ok = sem("var_ok")
        xs_ok = sem("xs_ok")
        n_lo_ok = sem("n_lo_ok")
        xc_ok = sem("xc_ok")
        clamp_ok = sem("clamp_ok")
        scan_ok = sem("scan_ok")
        d_ok = sem("d_ok")
        pool_y = sem("pool_y")
        lmul_ok = sem("lmul_ok")
        lru_y = sem("lru_y")
        ys_lo_ok, wo_lo_ok = sem("ys_lo_ok"), sem("wo_lo_ok")
        op_evac = sem("op_evac")
        hf_ok, hT_lo_ok = sem("hf_ok"), sem("hT_lo_ok")
        d_evac = sem("d_evac")
        fin_rstd_ok = sem("fin_rstd_ok")
        fin_ok = sem("fin_ok")
        vT_ok = sem("vT_ok")
        xT_ok = sem("xT_ok")
        proj_ok = sem("proj_ok")
        gates_ok = sem("gates_ok")
        poolmm_ok = sem("poolmm_ok")
        ss_ok = sem("ss_ok")
        op_ok = sem("op_ok")
        gu_ok = sem("gu_ok")
        down_ok = sem("down_ok")

        VEC, row = {}, 0
        for name, rows in (("conv_w", TAPS * GT), ("conv_b", GT), ("b_a", GT), ("b_i", GT), ("lam", GT),
                           ("pool_scale", GT), ("gn_pool", GT), ("gn_lru", GT)):
            VEC[name] = row
            row += rows
        NROWS = row

        def v(name, j):
            return vec[:, VEC[name] + j:VEC[name] + j + 1]

        def f32(ap):
            return ap.bitcast(F32)

        def cols(c):
            return slice(c * P, (c + 1) * P)

        def half(i):
            return slice(i * HALF, (i + 1) * HALF)

        def padded(i):
            return slice(PAD + i * HALF, PAD + (i + 1) * HALF)

        ssum = [ig, ag]
        wo_raw = w_raw[:].rearrange("p s k n -> p (s k n)").rearrange("p (k n) -> p k n", k=GT)
        ys_hi = [w_hi[0][:, GT * s:GT * (s + 1), :] for s in range(2)]
        ys_lo = [w_lo[0][:, GT * s:GT * (s + 1), :] for s in range(2)]

        t2 = t2b[:]
        ig_ring = [sumA[:, PAD:], ig[:]]
        down_bank = [*pg, *pt]
        BATCHES = ((0, 1), (1, 2), (2, 4), (4, TT))
        NB = len(BATCHES)
        FIN_G = TT - 2
        UNITS = [(0, 0), (1, 0), (0, 1), (1, 1)] + [(c, i) for c in range(2, NC_IN) for i in range(2)]

        def position(c, i):
            return UNITS.index((c, i))

        def after(c):
            return max(position(c, 0), position(c, 1)) + 1
        NCONST = 2 + 4 + PAD

        block = ctx.enter_context(nc.Block())

        @block.sync
        def _(sp_q):
            def load_w_in(c):
                if c >= 2:
                    sp_q.wait_ge(w_hi_ok, c - 1)
                    sp_q.wait_ge(w_lo_ok, c - 1)
                sp_q.dma_start(w_raw[:, c % 2], w_in_v[:, :, cols(COLS[c])]).then_inc(w_in_slot[c % 2], 16)

            def load_x(t):
                sp_q.dma_start(h[:, t, :], xf[cols(t), :]).then_inc(x_in[t], 16)

            load_x(0)
            sp_q.dma_start(g_row[:], ln1_g.to_broadcast([P, D])).then_inc(grow_in, 16)
            load_x(1)
            load_x(2)
            load_x(3)
            load_w_in(0)
            load_x(4)
            load_x(5)
            load_w_in(1)
            load_x(6)
            load_x(7)
            for name, src in (("conv_w", conv_w[0].rearrange("t (j p) -> (t j) p", p=P)),
                              ("conv_b", conv_b.rearrange("o (j p) -> (o j) p", p=P)),
                              ("b_a", b_a.rearrange("o (j p) -> (o j) p", p=P)),
                              ("b_i", b_i.rearrange("o (j p) -> (o j) p", p=P)),
                              ("lam", lam.rearrange("o (j p) -> (o j) p", p=P)),
                              ("pool_scale", pool_scale.rearrange("o (j p) -> (o j) p", p=P)),
                              ("gn_pool", gn_pool_g.rearrange("o (j p) -> (o j) p", p=P)),
                              ("gn_lru", gn_lru_g.rearrange("o (j p) -> (o j) p", p=P))):
                sp_q.dma_start(vrows[VEC[name]:VEC[name] + src.shape[0], :], src).then_inc(rows_in, 16)
            sp_q.wait_ge(zeroed, 2)
            for wt, dst in ((w_a, gate_w[0]), (w_i, gate_w[1])):
                blocks = wt[0].rearrange("(j b) c d -> b c j d", b=P // HD)
                for b in range(P // HD):
                    s = slice(b * HD, (b + 1) * HD)
                    sp_q.dma_start(dst[s, :, s], blocks[b]).then_inc(small_in, 16)
            sp_q.dma_start(pool_ws[:], pool_w[0].rearrange("g c d -> c g d")).then_inc(small_in, 16)
            for c in range(2, NC_IN):
                load_w_in(c)
            for q in range(4):
                if q == 0:
                    sp_q.wait_ge(w_hi_ok, NC_IN)
                    sp_q.wait_ge(w_lo_ok, NC_IN)
                else:
                    sp_q.wait_ge(wo_hi_ok, q)
                    sp_q.wait_ge(wo_lo_ok, q)
                g, ch = q // 2, q % 2
                sp_q.dma_start(wo_raw, w_out_v[:, GT * g:GT * (g + 1), ch * 512:(ch + 1) * 512]).then_inc(wo_in, 16)
            sp_q.wait_ge(xs_ok, TT)
            sp_q.dma_start(g_row[:], ln2_g.to_broadcast([P, D])).then_inc(grow_in, 16)

            def load_gu(i, s):
                col = (i * CH + s) * P
                sp_q.dma_start(gu_raw[s][:, 0], w_gate_v[:, :, bass.ds(col, P)]).then_inc(gu_in[s], 16)
                sp_q.dma_start(gu_raw[s][:, 1], w_up_v[:, :, bass.ds(col, P)]).then_inc(gu_in[s], 16)

            def load_dn(i):
                sp_q.dma_start(dn_raw[:], w_down_v[:, bass.ds(i * CH, CH), :]).then_inc(dn_in, 16)

            sp_q.wait_ge(ys_hi_ok, 2 * TT)
            sp_q.wait_ge(ys_lo_ok, 2 * TT)
            load_gu(0, 0)
            load_gu(0, 1)
            sp_q.wait_ge(wo_hi_ok, 4)
            sp_q.wait_ge(wo_lo_ok, 4)
            load_dn(0)
            sp_q.wait_ge(xs_ok, 2 * TT)
            sp_q.dma_start(g_row[:], lnf_g.rearrange("(o d) -> o d", o=1).to_broadcast([P, D])).then_inc(grow_in, 16)

            with sp_q.Fori(1, NCH) as i:
                for s in range(CH):
                    sp_q.wait_ge(gu_hi_ok, i * CH - CH + s + 1)
                    sp_q.wait_ge(gu_lo_ok, i * CH - CH + s + 1)
                    load_gu(i, s)
                sp_q.wait_ge(dn_hi_ok, i)
                sp_q.wait_ge(dn_lo_ok, i)
                load_dn(i)
            for m in range(TT):
                if m < FIN_G:
                    sp_q.wait_ge(fin_g_ok, m + 1)
                else:
                    sp_q.wait_ge(fin_ok, m - FIN_G + 1)
                sp_q.dma_start(outf[cols(m), :], fin[m][:]).then_inc(stored, 16)
            sp_q.wait_ge(stored, 16 * TT)

        @block.gpsimd
        def _(pool):
            steps = 0

            def step(ins):
                nonlocal steps
                steps += 1
                ins.then_inc(zeroed, 1)
                pool.wait_ge(zeroed, steps)

            step(pool.memset(gate_w[0][:], 0.0))
            step(pool.memset(gate_w[1][:], 0.0))
            step(pool.memset(ident[:], 0.0))
            pool.affine_select(out=ident[:], in_=ident[:], compare_op=ALU.not_equal, fill=1.0, base=0,
                               pattern=[[-1, P]], channel_multiplier=1).then_inc(consts, 1)
            pool.memset(ones[:], 1.0).then_inc(consts, 1)
            for b in (*ub, sumA, sumB):
                pool.memset(b[:, 0:PAD], 0.0).then_inc(consts, 1)
            for t in range(PAD):
                pool.memset(invp[:, t:t + 1], 1.0 / (t + 1)).then_inc(consts, 1)

            def split_w(c):
                pool.wait_ge(w_hi_ok, c + 1)
                pool.tensor_tensor(w_lo[c % 2][:], w_raw[:, c % 2], f32(w_hi[c % 2][:]), ALU.subtract)\
                    .then_inc(w_lo_ok, 1)

            split_w(0)
            split_w(1)
            for c in range(NC_IN):
                j = c - 2
                if 0 <= j < GT:
                    pool.wait_ge(gate_evac, 4 * j + 4)
                    pool.tensor_tensor(ig_ring[j % 2], ig_ring[j % 2], xc[j % 2][:], ALU.mult).then_inc(ix_ok, 1)
                p = c - POOL0 - 2
                if 1 <= p < GT:
                    pool.wait_ge(psq_ok, 2 * p + 2)
                    if p >= 2:
                        pool.wait_ge(ssum_ok, p - 1)
                    pool.tensor_tensor(ssum[0][:], ssum[0][:], rg[:], ALU.add).then_inc(ssum_ok, 1)
                if c + 2 < NC_IN:
                    split_w(c + 2)

            def add_lru_squares(g):
                pool.wait_ge(lsq_ok, g + 1)
                if g >= 2:
                    pool.wait_ge(ssum_ok, GT - 1 + g - 1)
                pool.tensor_tensor(ssum[1][:], ssum[1][:], rg[:], ALU.add).then_inc(ssum_ok, 1)

            add_lru_squares(1)
            for n in range(4 * TT):
                pool.wait_ge(ys_hi_ok, n + 1)
                pool.tensor_tensor(ys_lo[n % 2], y[n // (2 * TT)][:, :, cols(n % TT)], f32(ys_hi[n % 2]),
                                   ALU.subtract).then_inc(ys_lo_ok, 1)
                if n == 1:
                    add_lru_squares(2)
                if n == 2:
                    add_lru_squares(3)

            def split_gu(n, s):
                pool.wait_ge(gu_hi_ok, n + 1)
                pool.tensor_tensor(gu_lo[s][:], gu_raw[s][:], f32(gu_hi[s][:]), ALU.subtract).then_inc(gu_lo_ok, 1)

            def split_dn(i):
                pool.wait_ge(dn_hi_ok, i + 1)
                pool.tensor_tensor(dn_lo[:], dn_raw[:], f32(dn_hi[:]), ALU.subtract).then_inc(dn_lo_ok, 1)

            for s in range(CH):
                split_gu(s, s)
            with pool.Fori(0, NCH - 1) as i:
                split_dn(i)
                for s in range(CH):
                    split_gu((i + 1) * CH + s, s)
            split_dn(NCH - 1)
            pool.wait_ge(grow_in, 48)
            for m in range(FIN_G):
                pool.wait_ge(fin_n_ok, m + 1)
                pool.tensor_tensor(fin[m][:], fin[m][:], g_row[:], ALU.mult).then_inc(fin_g_ok, 1)

        @block.scalar
        def _(act):
            def split_w(c):
                act.wait_ge(w_in_slot[c % 2], 16 * (c // 2 + 1))
                if c >= 2:
                    act.wait_ge(proj_ok, after(c - 2))
                act.copy(w_hi[c % 2][:], w_raw[:, c % 2]).then_inc(w_hi_ok, 1)

            def nT_hi_part(n):
                for b in range(2):
                    act.wait_ge(xT_ok, 2 * n + b + 1)
                    act.copy(nT_hi[:, 4 * b:4 * b + 4, cols(n % TT)],
                             pt[b][:].rearrange("p (k n) -> p k n", k=4)).then_inc(n_hi_ok, 1)

            def squares(n, t, scratch):
                if n > 0:
                    act.wait_ge(sq_ok, n)
                act.activation(scratch, h[:, t, :], ACT.Square, accum_out=ssq[:, n:n + 1]).then_inc(sq_ok, 1)

            def norm_sqrt(n, lo, hi):
                act.wait_ge(var_ok, n)
                act.activation(sd[:, lo:hi], var[:, lo:hi], ACT.Sqrt).then_inc(sd_ok, 1)

            def x_squares(t):
                act.wait_ge(x_in[t], 16)
                squares(t, t, sumA[:, PAD:])

            act.wait_ge(consts, NCONST)
            act.activation(early[:], ones[:], ACT.Sqrt)
            for b in range(NB - 1):
                for t in range(*BATCHES[b]):
                    x_squares(t)
                norm_sqrt(b + 1, *BATCHES[b])
            for t in range(4):
                nT_hi_part(t)
                x_squares(4 + t)
                if t == 1:
                    split_w(0)
            norm_sqrt(NB, *BATCHES[NB - 1])
            split_w(1)
            act.wait_ge(vT_ok, 1)
            act.copy(vec[:, 0:NROWS], pg[0][:, 0:NROWS]).then_inc(vec_ok, 1)
            for t in range(4, TT):
                nT_hi_part(t)
            act.wait_ge(abs_ok, 1)
            act.activation(sp[:, 1], sp[:, 0], ACT.Exp, scale=-1.0).then_inc(exp_ok, 1)

            def evacuate(c, i):
                u = position(c, i)
                act.wait_ge(proj_ok, u + 1)
                if i == 0 and c >= 2:
                    if c < POOL0 + 2:
                        act.wait_ge(xc_ok, c - 1)
                    elif c < GATE0 + 2:
                        act.wait_ge(d_ok, c - 1 - POOL0)
                    else:
                        act.wait_ge(lmul_ok, c - 1 - GATE0)
                if c < POOL0:
                    if i == 0 and c == 0:
                        act.wait_ge(xT_ok, 2 * TT)
                        act.wait_ge(vec_ok, 1)
                    if i == 0 and c >= 2:
                        act.wait_ge(gates_ok, 4 * (c - 1))
                        act.wait_ge(ix_ok, c - 1)
                    act.copy(ub[c % 2][:, padded(i)], pj[u % 4][:])
                    act.activation(xc[c % 2][:, half(i)], pj[u % 4][:], ACT.Identity,
                                   bias=v("conv_b", c), scale=v("conv_w", (TAPS - 1) * GT + c)).then_inc(u_ok, 1)
                elif c < GATE0:
                    act.copy(ub[c % 2][:, padded(i)], pj[u % 4][:]).then_inc(u_ok, 1)
                else:
                    act.activation(ub[c % 2][:, padded(i)], pj[u % 4][:], ACT.Gelu_apprx_tanh).then_inc(u_ok, 1)

            def sigmoids(j, i):
                for g, (dst, bias) in enumerate(((rg[:], "b_a"), (ig_ring[j % 2], "b_i"))):
                    n = 4 * j + 2 * i + g
                    act.wait_ge(gates_ok, n + 1)
                    if i == 0 and g == 0 and j > 0:
                        act.wait_ge(a_ok, j)
                    if i == 0 and g == 1 and j > 1:
                        act.wait_ge(scan_ok, j - 1)
                    act.activation(dst[:, half(i)], pg[n % 2][:], ACT.Sigmoid, bias=v(bias, j)).then_inc(gate_evac, 1)

            def decay(j):
                act.wait_ge(gate_evac, 4 * j + 4)
                if j == 0:
                    act.wait_ge(decay_ok, 2)
                if j > 0:
                    act.wait_ge(scan_ok, j)
                act.activation(t2, rg[:], ACT.Tanh, scale=sp[:, 6, j:j + 1]).then_inc(t2_ok, 1)
                act.activation(ag[:], rg[:], ACT.Exp, scale=sp[:, 7, j:j + 1]).then_inc(a_ok, 1)

            def root(j):
                act.wait_ge(clamp_ok, j + 1)
                act.activation(t2, t2, ACT.Sqrt).then_inc(sqrt_ok, 1)

            def pool_squares(p):
                for i in range(2):
                    w = 2 * p + i
                    act.wait_ge(poolmm_ok, w + 1)
                    if w == 0:
                        act.wait_ge(scan_ok, GT)
                    if p >= 2 and i == 0:
                        act.wait_ge(ssum_ok, p - 1)
                    dst = ssum[0] if p == 0 else rg
                    act.activation(dst[:, half(i)], pg[w % 2][:], ACT.Square, scale=v("pool_scale", p))\
                        .then_inc(psq_ok, 1)

            def lru_squares(g):
                act.wait_ge(lmul_ok, g + 1)
                if g >= 1:
                    act.wait_ge(ssum_ok, GT - 1 + g - 1)
                dst = ssum[1] if g == 0 else rg
                act.activation(dst[:], y[1][:, g, :], ACT.Square).then_inc(lsq_ok, 1)

            def split_wo(q):
                act.wait_ge(wo_in, 16 * (q + 1))
                if q == 0:
                    act.wait_ge(poolmm_ok, 2 * GT)
                elif q == 1:
                    act.wait_ge(ss_ok, 2)
                else:
                    act.wait_ge(op_ok, TT * (q - 1))
                act.copy(wo_hi[q % 2][:], wo_raw).then_inc(wo_hi_ok, 1)

            def group_sqrt(g):
                act.wait_ge(var_ok, NB + g + 1)
                act.activation(gsd[:, g * TT:(g + 1) * TT], gvar[:, g * TT:(g + 1) * TT], ACT.Sqrt).then_inc(sd_ok, 1)

            def y_hi_part(n):
                if n == 0:
                    act.wait_ge(proj_ok, 2 * (NC_IN - 1))
                    act.wait_ge(pool_y, 2 * GT)
                if n == 2 * TT:
                    act.wait_ge(lru_y, GT)
                if n >= 2:
                    act.wait_ge(op_ok, n - 1)
                act.copy(ys_hi[n % 2], y[n // (2 * TT)][:, :, cols(n % TT)]).then_inc(ys_hi_ok, 1)

            for c, i in UNITS[0:4]:
                evacuate(c, i)
            split_w(2)
            split_w(3)
            sigmoids(0, 0)
            for c in range(2, NC_IN):
                if 0 <= c - 2 < GT:
                    sigmoids(c - 2, 1)
                    decay(c - 2)
                evacuate(c, 0)
                if 0 <= c - 2 < GT:
                    root(c - 2)
                if 0 <= c - POOL0 - 2 < GT:
                    pool_squares(c - POOL0 - 2)
                if c == NC_IN - 1:
                    y_hi_part(0)
                    y_hi_part(1)
                    group_sqrt(0)
                evacuate(c, 1)
                if c + 2 < NC_IN:
                    split_w(c + 2)
                if 0 <= c - 1 < GT:
                    sigmoids(c - 1, 0)
                if c - 1 >= GATE0:
                    lru_squares(c - 1 - GATE0)
                if c == NC_IN - 2:
                    split_wo(0)

            def split_gu(i, s):
                act.wait_ge(gu_in[s], (i + 1) * 32)
                if isinstance(i, int) and i == 0:
                    act.wait_ge(op_ok, TT * (3 + s))
                else:
                    act.wait_ge(gu_ok, (i - 1) * (2 * CH) + (2 * s + 2))
                act.copy(gu_hi[s][:], gu_raw[s][:]).then_inc(gu_hi_ok, 1)

            lru_squares(GT - 1)
            for n in range(2, 3 * TT + 1):
                y_hi_part(n)
                if n == 5:
                    split_wo(1)
                if n == 6:
                    group_sqrt(1)
                if n == TT + 1:
                    split_wo(2)
                if n == 2 * TT + 1:
                    split_wo(3)
            for m in range(TT + 4):
                if m >= 4:
                    nT_hi_part(TT + m - 4)
                if m < TT - 1:
                    y_hi_part(3 * TT + m + 1)
                if m == 1:
                    split_gu(0, 0)
                if 1 <= m <= TT:
                    act.wait_ge(op_evac, 3 * TT + m)
                    squares(TT + m - 1, m - 1, ub[0][:, PAD:])
                    norm_sqrt(NB + 2 + m, TT + m - 1, TT + m)
                if m == TT + 1:
                    split_gu(0, 1)

            def swiglu(i, s, hh):
                g = i * (2 * CH) + (2 * s + hh)
                act.wait_ge(gu_ok, g + 1)
                if not (isinstance(i, int) and i == 0 and s == 0):
                    act.wait_ge(hf_ok, g - 1)
                act.activation(silu[hh][:], pj[2 * hh][:], ACT.Silu).then_inc(silu_ok, 1)
                act.wait_ge(hf_ok, g + 1)
                act.copy(hT_hi[:, s, half(hh)], hf[hh][:]).then_inc(hT_hi_ok, 1)

            def chunk(i, last=False):
                act.wait_ge(dn_in, (i + 1) * 16)
                if isinstance(i, int) and i == 0:
                    act.wait_ge(xT_ok, 4 * TT)
                    act.wait_ge(op_ok, 4 * TT)
                else:
                    act.wait_ge(down_ok, i * (NH * TT))
                act.copy(dn_hi[:], dn_raw[:]).then_inc(dn_hi_ok, 1)
                for s in range(CH):
                    for hh in range(2):
                        swiglu(i, s, hh)
                    if not last:
                        split_gu(i + 1, s)

            chunk(0)
            with act.Fori(1, NCH - 1) as i:
                chunk(i)
            chunk(NCH - 1, last=True)

            for m in range(TT):
                act.wait_ge(d_evac, NH * (TT * (NCH - 1) + m + 1))
                squares(2 * TT + m, m, fin_sq[:])
                norm_sqrt(NB + 2 + TT + m + 1, 2 * TT + m, 2 * TT + m + 1)
                if 1 <= m <= FIN_G:
                    act.wait_ge(fin_rstd_ok, m)
                    act.activation(fin[m - 1][:], h[:, m - 1, :], ACT.Copy,
                                   scale=rstd[:, 2 * TT + m - 1:2 * TT + m]).then_inc(fin_n_ok, 1)

        @block.vector
        def _(dve):
            steps = finished = 0

            def step(ins):
                nonlocal steps
                steps += 1
                ins.then_inc(dve_step, 1)
                dve.wait_ge(dve_step, steps)

            def rsqrt(var_, sd_, out_, tmp_, ready=None):
                step(dve.reciprocal(out_, sd_))
                step(dve.tensor_tensor(tmp_, out_, out_, ALU.mult))
                step(dve.tensor_tensor(tmp_, tmp_, var_, ALU.mult))
                step(dve.tensor_scalar(tmp_, tmp_, -0.5, 1.5, ALU.mult, ALU.add))
                if ready is None:
                    step(dve.tensor_tensor(out_, out_, tmp_, ALU.mult))
                else:
                    nonlocal finished
                    finished += 1
                    dve.tensor_tensor(out_, out_, tmp_, ALU.mult).then_inc(ready, 1)
                    dve.wait_ge(ready, finished)

            def variance(lo, hi):
                dve.wait_ge(sq_ok, hi)
                dve.tensor_scalar(var[:, lo:hi], ssq[:, lo:hi], 1.0 / D, EPS, ALU.mult, ALU.add).then_inc(var_ok, 1)

            def norm_rsqrt(n, lo, hi, ready=None):
                dve.wait_ge(sd_ok, n)
                rsqrt(var[:, lo:hi], sd[:, lo:hi], rstd[:, lo:hi], tmp[:, lo:hi], ready)

            def normalise(n, xs):
                if n % TT >= 2:
                    dve.wait_ge(xT_ok, 2 * (n - 1))
                if n == 0:
                    dve.wait_ge(grow_in, 16)
                if n == TT:
                    dve.wait_ge(grow_in, 32)
                    dve.wait_ge(proj_ok, 2 * NC_IN)
                dve.scalar_tensor_tensor(out=xs[n % 2][:], in0=h[:, n % TT, :], scalar=rstd[:, n:n + 1],
                                         in1=g_row[:], op0=ALU.mult, op1=ALU.mult).then_inc(xs_ok, 1)

            def nT_lo_part(n):
                for b in range(2):
                    dve.wait_ge(n_hi_ok, 2 * n + b + 1)
                    dst = (slice(None), slice(4 * b, 4 * b + 4), cols(n % TT))
                    dve.tensor_tensor(nT_lo[dst], pt[b][:].rearrange("p (k n) -> p k n", k=4), f32(nT_hi[dst]),
                                      ALU.subtract).then_inc(n_lo_ok, 1)

            for b, (lo, hi) in enumerate(BATCHES):
                if b == NB - 1:
                    nT_lo_part(2)
                    nT_lo_part(3)
                variance(lo, hi)
                norm_rsqrt(b + 1, lo, hi)
                for t in range(lo, hi):
                    if b == NB - 2:
                        nT_lo_part(t - 2)
                    normalise(t, xc)
                    if b == NB - 1 and t > lo:
                        nT_lo_part(t - 1)
            nT_lo_part(TT - 1)
            dve.wait_ge(vec_ok, 1)
            L = vec[:, VEC["lam"]:VEC["lam"] + GT]
            dve.scalar_tensor_tensor(out=sp[:, 0], in0=L, scalar=-1.0, in1=L, op0=ALU.mult, op1=ALU.max)\
                .then_inc(abs_ok, 1)
            dve.wait_ge(exp_ok, 1)
            e, s1, s2, acc, pos = (sp[:, k] for k in range(1, 6))
            step(dve.tensor_scalar(s1, e, 2.0, None, ALU.add))
            step(dve.reciprocal(s1, s1))
            step(dve.tensor_tensor(s1, s1, e, ALU.mult))
            step(dve.tensor_tensor(s2, s1, s1, ALU.mult))
            step(dve.tensor_scalar(acc, s2, 1.0 / 19, None, ALU.mult))
            for k in range(17, 1, -2):
                step(dve.scalar_tensor_tensor(out=acc, in0=acc, scalar=1.0 / k, in1=s2, op0=ALU.add, op1=ALU.mult))
            step(dve.scalar_tensor_tensor(out=acc, in0=acc, scalar=1.0, in1=s1, op0=ALU.add, op1=ALU.mult))
            step(dve.tensor_scalar(pos, L, -1.0, 0.0, ALU.mult, ALU.max))
            step(dve.scalar_tensor_tensor(out=acc, in0=acc, scalar=2.0, in1=pos, op0=ALU.mult, op1=ALU.add))
            dve.tensor_scalar(sp[:, 6], acc, LRU_C / 2, None, ALU.mult).then_inc(decay_ok, 1)
            dve.tensor_scalar(sp[:, 7], acc, -LRU_C, None, ALU.mult).then_inc(decay_ok, 1)

            def convolve(j):
                dve.wait_ge(u_ok, after(j))
                for k in range(TAPS - 1):
                    off = PAD - (TAPS - 1) + k
                    ins = dve.scalar_tensor_tensor(out=xc[j % 2][:], in0=ub[j % 2][:, off:off + S],
                                                   scalar=v("conv_w", k * GT + j), in1=xc[j % 2][:],
                                                   op0=ALU.mult, op1=ALU.add)
                    if k < TAPS - 2:
                        step(ins)
                ins.then_inc(xc_ok, 1)

            def recur(j):
                dve.wait_ge(t2_ok, j + 1)
                dve.tensor_scalar(t2, t2, 0.0, None, ALU.max).then_inc(clamp_ok, 1)
                dve.wait_ge(sqrt_ok, j + 1)
                dve.wait_ge(a_ok, j + 1)
                step(dve.scalar_tensor_tensor(out=t2, in0=ag[:], scalar=1.0, in1=t2, op0=ALU.add, op1=ALU.mult))
                dve.wait_ge(ix_ok, j + 1)
                b = ig_ring[j % 2]
                step(dve.tensor_tensor(b, b, t2, ALU.mult))
                dve.tensor_tensor_scan(y[1][:, j, :], ag[:], b, 0.0, ALU.mult, ALU.add).then_inc(scan_ok, 1)

            def window_mean(p):
                w, src = WINDOWS[p], ub[p % 2]
                dve.wait_ge(u_ok, after(POOL0 + p))
                if p == 0:
                    dve.wait_ge(scan_ok, GT - 1)
                cur, nxt, other = src, sumA, sumB
                for k in range(p + 1):
                    lag = 1 << k
                    step(dve.tensor_tensor(nxt[:, PAD:], cur[:, PAD:], cur[:, PAD - lag:PAD - lag + S], ALU.add))
                    cur, nxt, other = nxt, other, nxt
                if p >= 2:
                    dve.wait_ge(poolmm_ok, 2 * (p - 1))
                d = xc[p % 2]
                step(dve.scalar_tensor_tensor(out=d[:], in0=cur[:, PAD:], scalar=1.0 / w, in1=src[:, PAD:],
                                              op0=ALU.mult, op1=ALU.subtract))
                step(dve.scalar_tensor_tensor(out=dfix[:], in0=invp[:], scalar=1.0 / w, in1=cur[:, PAD:2 * PAD],
                                              op0=ALU.max, op1=ALU.mult))
                dve.tensor_tensor(d[:, 0:PAD], dfix[:], src[:, PAD:2 * PAD], ALU.subtract).then_inc(d_ok, 1)

            def pool_output(p):
                for i in range(2):
                    w = 2 * p + i
                    dve.wait_ge(psq_ok, w + 1)
                    dve.tensor_scalar(y[0][:, p, half(i)], pg[w % 2][:], v("pool_scale", p), v("gn_pool", p),
                                      ALU.mult, ALU.mult).then_inc(pool_y, 1)

            def gate_lru(g):
                c = GATE0 + g
                dve.wait_ge(u_ok, after(c))
                dve.tensor_tensor(y[1][:, g, :], y[1][:, g, :], ub[c % 2][:, PAD:], ALU.mult).then_inc(lmul_ok, 1)

            def lru_gain(g):
                dve.wait_ge(lsq_ok, g + 1)
                dve.tensor_scalar(y[1][:, g, :], y[1][:, g, :], v("gn_lru", g), None, ALU.mult).then_inc(lru_y, 1)

            def split_wo(q):
                dve.wait_ge(wo_hi_ok, q + 1)
                dve.tensor_tensor(wo_lo[q % 2][:], wo_raw, f32(wo_hi[q % 2][:]), ALU.subtract).then_inc(wo_lo_ok, 1)

            def group_variance(g):
                dve.wait_ge(ss_ok, g + 1)
                dve.tensor_scalar(gvar[:, g * TT:(g + 1) * TT], pt[g][:, 0:TT], 1.0 / GW, EPS, ALU.mult, ALU.add)\
                    .then_inc(var_ok, 1)

            def group_rsqrt(g):
                dve.wait_ge(sd_ok, NB + g + 1)
                t = slice(g * TT, (g + 1) * TT)
                rsqrt(gvar[:, t], gsd[:, t], grstd[:, t], tmp[:, 0:TT])

            dve.wait_ge(consts, NCONST)
            for c in range(NC_IN):
                if 0 <= c - 2 < GT:
                    recur(c - 2)
                if 0 <= c - POOL0 - 2 < GT:
                    pool_output(c - POOL0 - 2)
                if c < POOL0:
                    convolve(c)
                elif c < GATE0:
                    window_mean(c - POOL0)
                else:
                    if c == NC_IN - 1:
                        group_variance(0)
                        group_rsqrt(0)
                    gate_lru(c - GATE0)
                    if c > GATE0:
                        lru_gain(c - GATE0 - 1)
                if c == NC_IN - 2:
                    split_wo(0)

            def add_projection(n):
                m, ch, g = n % TT, (n // TT) % 2, n // (2 * TT)
                dst = h[:, m, ch * 512:(ch + 1) * 512]
                dve.wait_ge(op_ok, n + 1)
                dve.scalar_tensor_tensor(out=dst, in0=pj[n % 4][:], scalar=grstd[:, g * TT + m:g * TT + m + 1],
                                         in1=dst, op0=ALU.mult, op1=ALU.add).then_inc(op_evac, 1)

            for n in range(3 * TT):
                if n == 1:
                    lru_gain(GT - 1)
                add_projection(n)
                if n == 5:
                    split_wo(1)
                    group_variance(1)
                if n == 7:
                    group_rsqrt(1)
                if n == TT:
                    split_wo(2)
                if n == 2 * TT:
                    split_wo(3)
            for m in range(TT + 4):
                if m >= 4:
                    nT_lo_part(TT + m - 4)
                if m < TT:
                    add_projection(3 * TT + m)
                if 1 <= m <= TT:
                    variance(TT + m - 1, TT + m)
                if 2 <= m <= TT + 1:
                    norm_rsqrt(NB + 2 + m - 1, TT + m - 2, TT + m - 1)
                    normalise(TT + m - 2, xs2)

            def swiglu(i, s, hh):
                g = i * (2 * CH) + (2 * s + hh)
                dve.wait_ge(silu_ok, g + 1)
                if not (isinstance(i, int) and i == 0 and s == 0):
                    dve.wait_ge(hT_hi_ok, g - 1)
                dve.tensor_tensor(hf[hh][:], silu[hh][:], pj[2 * hh + 1][:], ALU.mult).then_inc(hf_ok, 1)
                dve.wait_ge(hT_hi_ok, g + 1)
                dve.tensor_tensor(hT_lo[:, s, half(hh)], hf[hh][:], f32(hT_hi[:, s, half(hh)]), ALU.subtract)\
                    .then_inc(hT_lo_ok, 1)

            def add_down(i, m):
                for ch in range(NH):
                    d = NH * m + ch
                    dst = h[:, m, ch * 512:(ch + 1) * 512]
                    dve.wait_ge(down_ok, i * (NH * TT) + (d + 1))
                    dve.tensor_tensor(dst, down_bank[d % 4][:], dst, ALU.add).then_inc(d_evac, 1)

            def chunk(i):
                for s in range(CH):
                    for hh in range(2):
                        swiglu(i, s, hh)

            chunk(0)
            for m in range(TT):
                add_down(0, m)
            with dve.Fori(1, NCH - 1) as i:
                chunk(i)
                for m in range(TT):
                    add_down(i, m)
            chunk(NCH - 1)

            for m in range(TT + 2):
                if m < TT:
                    add_down(NCH - 1, m)
                if m >= 2:
                    n = 2 * TT + m - 2
                    norm_rsqrt(NB + 2 + TT + m - 1, n, n + 1, fin_rstd_ok)
                    if m - 2 >= FIN_G:
                        dve.wait_ge(grow_in, 48)
                        dve.scalar_tensor_tensor(out=fin[m - 2][:], in0=h[:, m - 2, :], scalar=rstd[:, n:n + 1],
                                                 in1=g_row[:], op0=ALU.mult, op1=ALU.mult).then_inc(fin_ok, 1)
                if 1 <= m <= TT:
                    variance(2 * TT + m - 1, 2 * TT + m)

        @block.tensor
        def _(pe):
            def three_pass(bank, pairs, between=()):
                n = len(pairs)
                for k, (s_hi, s_lo, m_hi, m_lo) in enumerate(pairs):
                    pe.matmul(bank, s_lo, m_hi, start=(k == 0), stop=False)
                    pe.matmul(bank, s_hi, m_lo, start=False, stop=False)
                    ins = pe.matmul(bank, s_hi, m_hi, start=False, stop=(k == n - 1))
                    if k in between:
                        between[k]()
                return ins

            def transposes(n, xs):
                pe.wait_ge(xs_ok, n + 1)
                for b in range(2):
                    if n == TT:
                        pe.wait_ge(var_ok, NB + 2)
                    if n > 0:
                        pe.wait_ge(n_lo_ok, 2 * (n - 1) + b + 1)
                    for k in range(4):
                        ins = pe.transpose(pt[b][:, cols(k)], xs[n % 2][:, cols(4 * b + k)], ident[:])
                    ins.then_inc(xT_ok, 1)

            def project(c, i, between=()):
                u = position(c, i)
                if i == 0:
                    pe.wait_ge(w_lo_ok, c + 1)
                if c <= 1:
                    pe.wait_ge(n_lo_ok, TT * (i + 1))
                if u >= 4:
                    pe.wait_ge(u_ok, u - 3)
                s = c % 2
                three_pass(pj[u % 4][:], [(w_hi[s][:, k], w_lo[s][:, k], nT_hi[:, k, half(i)], nT_lo[:, k, half(i)])
                                          for k in range(KT)], between).then_inc(proj_ok, 1)

            def gates(j, i):
                if i == 0:
                    pe.wait_ge(xc_ok, j + 1)
                for g in range(2):
                    n = 4 * j + 2 * i + g
                    if n >= 2:
                        pe.wait_ge(gate_evac, n - 1)
                    if n == 0:
                        pe.wait_ge(vec_ok, 1)
                        pe.wait_ge(small_in, 16 * 5)
                    pe.matmul(pg[n % 2][:], gate_w[g][:, j], xc[j % 2][:, half(i)], start=True, stop=True)\
                        .then_inc(gates_ok, 1)

            def pool_product(p):
                pe.wait_ge(d_ok, p + 1)
                for i in range(2):
                    w = 2 * p + i
                    if p == 0:
                        pe.wait_ge(gate_evac, 4 * GT - 1 + i)
                    else:
                        pe.wait_ge(pool_y, w - 1)
                    pe.matmul(pg[w % 2][:], pool_ws[:, p], xc[p % 2][:, half(i)], start=True, stop=True)\
                        .then_inc(poolmm_ok, 1)

            def group_sums(g):
                pe.wait_ge(ssum_ok, (GT - 1) * (g + 1))
                for m in range(TT):
                    ins = pe.matmul(pt[g][:, m:m + 1], ssum[g][:, cols(m)], ones[:, 0:1], start=True, stop=True)
                ins.then_inc(ss_ok, 1)

            def project_out(n):
                q, s = n // TT, n % 2
                pe.wait_ge(ys_lo_ok, n + 1)
                if n % TT == 0:
                    pe.wait_ge(wo_lo_ok, q + 1)
                if n < 4:
                    pe.wait_ge(u_ok, 2 * NC_IN - 3 + n)
                else:
                    pe.wait_ge(op_evac, n - 3)
                three_pass(pj[n % 4][:], [(ys_hi[s][:, k], ys_lo[s][:, k], wo_hi[q % 2][:, k], wo_lo[q % 2][:, k])
                                          for k in range(GT)]).then_inc(op_ok, 1)

            pe.wait_ge(consts, NCONST)
            for t in range(4):
                transposes(t, xc)
            project(0, 0)
            pe.wait_ge(rows_in, 16 * 8)
            pe.transpose(pg[0][:, 0:NROWS], vrows[0:NROWS, :], ident[0:NROWS, 0:NROWS]).then_inc(vT_ok, 1)
            transposes(4, xc)
            project(1, 0, {2: lambda: transposes(5, xc), 5: lambda: transposes(6, xc)})
            transposes(7, xc)
            project(0, 1)
            project(1, 1)
            gates(0, 0)
            for c in range(2, NC_IN):
                project(c, 0)
                if 0 <= c - 2 < GT:
                    gates(c - 2, 1)
                if 0 <= c - POOL0 - 2 < GT:
                    pool_product(c - POOL0 - 2)
                if c == NC_IN - 1:
                    group_sums(0)
                project(c, 1)
                if 0 <= c - 1 < GT:
                    gates(c - 1, 0)

            for n in range(4 * TT):
                project_out(n)
                if n == 4:
                    group_sums(1)
                if n >= 3 * TT + 3:
                    transposes(TT + n - 3 * TT - 3, xs2)

            def gate_or_up(i, s, hh, w):
                return three_pass(pj[2 * hh + w][:], [(gu_hi[s][:, w, k], gu_lo[s][:, w, k], nT_hi[:, k, half(hh)],
                                                       nT_lo[:, k, half(hh)]) for k in range(KT)])

            def down(i):
                pe.wait_ge(dn_lo_ok, i + 1)
                for m in range(TT):
                    if m % (TT // 2) == 0:
                        pe.wait_ge(hT_lo_ok, i * (2 * CH) + (2 * CH - 1 + m // (TT // 2)))
                    for ch in range(NH):
                        d = NH * m + ch
                        if not (isinstance(i, int) and i == 0 and d < 4):
                            pe.wait_ge(d_evac, i * (NH * TT) + (d - 3))
                        n = slice(ch * 512, (ch + 1) * 512)
                        three_pass(down_bank[d % 4][:], [(hT_hi[:, s, cols(m)], hT_lo[:, s, cols(m)],
                                                          dn_hi[:, s, n], dn_lo[:, s, n]) for s in range(CH)])\
                            .then_inc(down_ok, 1)

            def chunk(i):
                first = isinstance(i, int) and i == 0
                for s in range(CH):
                    pe.wait_ge(gu_lo_ok, i * CH + (s + 1))
                    for hh in range(2):
                        g = i * (2 * CH) + (2 * s + hh)
                        if not (first and s == 0):
                            pe.wait_ge(hf_ok, g - 1)
                        elif hh == 0:
                            pe.wait_ge(op_evac, 4 * TT)
                            pe.wait_ge(n_lo_ok, 3 * TT)
                        else:
                            pe.wait_ge(n_lo_ok, 4 * TT)
                        gate_or_up(i, s, hh, 0)
                        if first and s == 0 and hh == 0:
                            transposes(2 * TT - 3, xs2)
                        gate_or_up(i, s, hh, 1).then_inc(gu_ok, 1)
                        if first and s == 0 and hh == 0:
                            transposes(2 * TT - 2, xs2)
                            transposes(2 * TT - 1, xs2)
                down(i)

            chunk(0)
            with pe.Fori(1, NCH - 1) as i:
                chunk(i)
            chunk(NCH - 1)


_INS = ["x", "ln1_g", "w_in", "pool_w", "pool_scale", "conv_w", "conv_b", "w_a", "b_a", "w_i", "b_i", "lam",
        "gn_pool_g", "gn_lru_g", "w_out", "ln2_g", "w_ffn_gate", "w_ffn_up", "w_ffn_down", "lnf_g"]


def kernel(**inputs):
    import numpy as np
    import concourse.bacc as bacc
    from concourse.bass_utils import run_bass_kernel_spmd

    nc = bacc.Bacc("TRN2", target_bir_lowering=False, num_devices=1)
    arrays, args = {}, []
    for name in _INS:
        a = np.ascontiguousarray(inputs[name])
        arrays[f"in_{name}"] = a
        args.append(nc.dram_tensor(f"in_{name}", a.shape, mybir.dt.from_np(a.dtype), kind="ExternalInput").ap())
    shape = inputs["x"].shape
    args.append(nc.dram_tensor("out_dram", shape, F32, kind="ExternalOutput").ap())
    hymba_pool_rglru_block(nc, *args)
    r = run_bass_kernel_spmd(nc, [arrays], core_ids=[0])
    return r.results[0]["out_dram"]
```
